# Optimizing a Trainium2 kernel written in Bass

```python
import jax, jax.numpy as jnp
from jax import lax
import numpy as np

D_MODEL = 1024
BATCH = 1
SEQ = 256
DEPTH = 2

GRID_W = 64
CTX_LEN = 256
D_A = 1024
CONV_W = 3
B_HEADS = 16
B_HEAD = 64
D_B = B_HEADS * B_HEAD
R_W = 64
R_A = 64
R_G = 128
GN_EPS = 64e-5
C_HEADS = 16
C_KV = 4
C_GROUP = C_HEADS // C_KV
HEAD_DIM = 64
WINDOW = 128
ATT_BLOCK = 128
ATT_SCALE = HEAD_DIM ** -0.5
ROPE_THETA = 10000.0
NEG_INF = -1e30
D_FF = 2816
NORM_EPS = 1e-6
N_BRANCH = 3
IN_SPLITS = (D_A, D_A, D_A, 3 * D_B, 2 * R_W, 2 * R_A, R_G,
             C_HEADS * HEAD_DIM, C_KV * HEAD_DIM, C_KV * HEAD_DIM, N_BRANCH * D_MODEL)
N_IN = sum(IN_SPLITS)

kernel_name = "hybrid_conv_rwkv7_swa_diffusion_trunk"

def rmsnorm(x, g):
    xf = x.astype(jnp.float32)
    y = xf * lax.rsqrt(jnp.mean(xf * xf, axis=-1, keepdims=True) + NORM_EPS)
    return (y * g.astype(jnp.float32)).astype(x.dtype)

def modulate(x, g, shift, scale):
    return rmsnorm(x, g) * (1.0 + scale) + shift

def dwconv3(x, w):
    xp = jnp.pad(x, ((0, 0), (1, 1), (0, 0)))
    return xp[:, :-2] * w[0] + xp[:, 1:-1] * w[1] + xp[:, 2:] * w[2]

def split_cols(p):
    offsets = tuple(int(o) for o in np.cumsum(IN_SPLITS)[:-1])
    return jnp.split(p, offsets, axis=-1)

def axial_rope_tables(seq, dtype):
    rows = seq // GRID_W
    t_row = jnp.broadcast_to(jnp.arange(rows)[:, None], (rows, GRID_W)).reshape(-1).astype(jnp.float32)
    t_col = jnp.broadcast_to(jnp.arange(GRID_W)[None, :], (rows, GRID_W)).reshape(-1).astype(jnp.float32)
    n_freq = HEAD_DIM // 4
    inv = ROPE_THETA ** (-jnp.arange(n_freq, dtype=jnp.float32) / n_freq)
    ang = jnp.stack([t_row[:, None] * inv, t_col[:, None] * inv], axis=1)
    return jnp.cos(ang).astype(dtype), jnp.sin(ang).astype(dtype)

def apply_rope2d(x, cos, sin):
    shp = x.shape
    xr = x.reshape(shp[:-1] + (2, 2, HEAD_DIM // 4))
    x1, x2 = xr[..., 0, :], xr[..., 1, :]
    c, s = cos[:, None], sin[:, None]
    out = jnp.stack([x1 * c - x2 * s, x1 * s + x2 * c], axis=-2)
    return out.reshape(shp)

def windowed_attention(q, k, v, kc, vc, sink):
    b, s = q.shape[:2]
    nb = s // ATT_BLOCK
    qb = q.reshape(b, nb, ATT_BLOCK, C_KV, C_GROUP, HEAD_DIM)

    def band(t):
        tp = jnp.pad(t, ((0, 0), (ATT_BLOCK, ATT_BLOCK), (0, 0), (0, 0)))
        tp = tp.reshape(b, nb + 2, ATT_BLOCK, C_KV, HEAD_DIM)
        return jnp.concatenate([tp[:, :-2], tp[:, 1:-1], tp[:, 2:]], axis=2)

    kb, vb = band(k), band(v)
    s_loc = jnp.einsum('bnqkgd,bnskd->bnkgqs', qb, kb).astype(jnp.float32)
    s_ctx = jnp.einsum('bnqkgd,bckd->bnkgqc', qb, kc).astype(jnp.float32)
    qi = jnp.arange(ATT_BLOCK)
    si = jnp.arange(3 * ATT_BLOCK)
    rel = si[None, :] - ATT_BLOCK - qi[:, None]
    kpos = jnp.arange(nb)[:, None, None] * ATT_BLOCK + si[None, None, :] - ATT_BLOCK
    mask = (jnp.abs(rel) <= WINDOW)[None] & (kpos >= 0) & (kpos < s)
    s_loc = jnp.where(mask[None, :, None, None], s_loc, NEG_INF)
    sink_b = jnp.broadcast_to(sink.reshape(C_KV, C_GROUP, 1, 1).astype(jnp.float32), s_ctx.shape[:-1] + (1,))
    probs = jax.nn.softmax(jnp.concatenate([s_loc, s_ctx, sink_b], axis=-1), axis=-1).astype(v.dtype)
    n_loc, n_ctx = 3 * ATT_BLOCK, kc.shape[1]
    o = (jnp.einsum('bnkgqs,bnskd->bnqkgd', probs[..., :n_loc], vb)
         + jnp.einsum('bnkgqc,bckd->bnqkgd', probs[..., n_loc:n_loc + n_ctx], vc))
    return o.reshape(b, s, C_HEADS * HEAD_DIM)

def context_attention(qc, kc, vc, sink):
    b, c = qc.shape[:2]
    qg = qc.reshape(b, c, C_KV, C_GROUP, HEAD_DIM)
    sc = jnp.einsum('bqkgd,bskd->bkgqs', qg, kc).astype(jnp.float32)
    sink_b = jnp.broadcast_to(sink.reshape(C_KV, C_GROUP, 1, 1).astype(jnp.float32), sc.shape[:-1] + (1,))
    probs = jax.nn.softmax(jnp.concatenate([sc, sink_b], axis=-1), axis=-1).astype(vc.dtype)
    o = jnp.einsum('bkgqs,bskd->bqkgd', probs[..., :c], vc)
    return o.reshape(b, c, C_HEADS * HEAD_DIM)

def rwkv_inputs(rkv, wl, al, gl, p):
    b, t = rkv.shape[:2]
    f = jnp.float32
    mu = p['rwkv_mu']
    shift_w = jnp.stack([mu[0], 1.0 - mu[0] - mu[1], mu[1]])
    r, k, v = jnp.split(dwconv3(rkv, shift_w), 3, axis=-1)
    wl = wl.reshape(b, t, 2, R_W)
    al = al.reshape(b, t, 2, R_A)
    w_pre = p['rwkv_w0'] + jnp.einsum('btdr,drc->btdc', jnp.tanh(wl), p['rwkv_w2'])
    w_log = -jax.nn.softplus(-w_pre.astype(f)) - 0.5
    decay = jnp.exp(-jnp.exp(w_log))
    a = jax.nn.sigmoid((p['rwkv_a0'] + jnp.einsum('btdr,drc->btdc', al, p['rwkv_a2'])).astype(f))
    g = jax.nn.sigmoid(gl) @ p['rwkv_g2']

    def heads(z):
        return z.reshape(z.shape[:-1] + (B_HEADS, B_HEAD))

    kk = heads((k * p['rwkv_k_k']).astype(f))
    kk = kk * lax.rsqrt(jnp.sum(kk * kk, axis=-1, keepdims=True) + 1e-12)
    k_d = heads(k.astype(f)[:, :, None] * (1.0 + (a - 1.0) * p['rwkv_k_a'].astype(f)))
    b_d = kk[:, :, None] * heads(a)
    return heads(r.astype(f)), heads(v.astype(f)), kk, heads(decay), k_d, b_d, g

def rwkv_scan(s0, r, v, kk, decay, k_d, b_d, emit):
    b, t = r.shape[:2]

    def both(z):
        return jnp.broadcast_to(z[:, :, None], (b, t, 2) + z.shape[2:])

    def to_dirs(z):
        return jnp.stack([z[:, :, 0], jnp.flip(z[:, :, 1], axis=1)], axis=0).transpose(2, 0, 1, 3, 4)

    xs = tuple(to_dirs(z) for z in (both(r), decay, k_d, both(v), both(-kk), b_d))

    def step(S, inp):
        rt, wt, kt, vt, at, bt = inp
        sa = jnp.einsum('dbhvk,dbhk->dbhv', S, at)
        S = S * wt[..., None, :] + sa[..., :, None] * bt[..., None, :] + vt[..., :, None] * kt[..., None, :]
        y = jnp.einsum('dbhvk,dbhk->dbhv', S, rt) if emit else None
        return S, y

    s_fin, ys = lax.scan(step, s0, xs)
    if not emit:
        return s_fin, None
    y = ys[:, 0] + jnp.flip(ys[:, 1], axis=0)
    return s_fin, y.transpose(1, 0, 2, 3)

def rwkv_branch(y, r, v, k_d, g, p, dtype):
    b, t = y.shape[:2]
    mean = jnp.mean(y, axis=-1, keepdims=True)
    var = jnp.mean(jnp.square(y - mean), axis=-1, keepdims=True)
    gn = ((y - mean) * lax.rsqrt(var + GN_EPS)).reshape(b, t, D_B) * p['rwkv_ln_g'] + p['rwkv_ln_b']
    bonus = jnp.sum(jnp.sum(r[:, :, None] * k_d * p['rwkv_r_k'], axis=-1, keepdims=True) * v[:, :, None], axis=2)
    return ((gn + bonus.reshape(b, t, D_B)) * g).astype(dtype)

def short_conv(bg, cg, xin, conv_w):
    return bg * dwconv3(cg * xin, conv_w)

def merge_branches(ya, yb, yc, gates, p):
    ga, gb, gc = jnp.split(jax.nn.sigmoid(gates), N_BRANCH, axis=-1)
    m = ga * (ya @ p['a_out_w']) + gb * (yb @ p['rwkv_out_w']) + gc * (yc @ p['attn_out_w'])
    return m @ p['w_o']

def conv_ffn(h, p):
    u = dwconv3(h @ p['ffn_up'], p['ffn_conv'])
    ug, uv = jnp.split(u, 2, axis=-1)
    return (jax.nn.silu(ug) * uv) @ p['ffn_down']

def trunk_layer(xc, xl, c, c_ctx, cos, sin, p, ctx_out):
    b = xl.shape[0]
    dt = xl.dtype
    mod_l = jnp.split((jax.nn.silu(c) @ p['ada_w'] + p['ada_b'])[:, None, :], 6, axis=-1)
    mod_c = jnp.split(jax.nn.silu(c_ctx) @ p['ada_w'] + p['ada_b'], 6, axis=-1)
    hl = modulate(xl, p['norm1_g'], mod_l[0], mod_l[1])
    hc = modulate(xc, p['norm1_g'], mod_c[0], mod_c[1])
    (ab_l, ac_l, ax_l, rkv_l, wl_l, al_l, gl_l, q_l, k_l, v_l, gate_l) = split_cols(hl @ p['w_in'])
    (ab_c, ac_c, ax_c, rkv_c, wl_c, al_c, gl_c, q_c, k_c, v_c, gate_c) = split_cols(hc @ p['w_in'])

    def heads_q(z):
        return z.reshape(z.shape[:2] + (C_HEADS, HEAD_DIM))

    def heads_kv(z):
        return z.reshape(z.shape[:2] + (C_KV, HEAD_DIM))

    kc, vc = heads_kv(k_c), heads_kv(v_c)
    ql = apply_rope2d(heads_q(q_l), cos, sin) * ATT_SCALE
    kl = apply_rope2d(heads_kv(k_l), cos, sin)
    att_l = windowed_attention(ql, kl, heads_kv(v_l), kc, vc, p['attn_sink'])

    r_c, vr_c, kk_c, dec_c, kd_c, bd_c, g_c = rwkv_inputs(rkv_c, wl_c, al_c, gl_c, p)
    s0 = jnp.zeros((2, b, B_HEADS, B_HEAD, B_HEAD), jnp.float32)
    s_ctx, y_rc = rwkv_scan(s0, r_c, vr_c, kk_c, dec_c, kd_c, bd_c, ctx_out)
    r_l, vr_l, kk_l, dec_l, kd_l, bd_l, g_l = rwkv_inputs(rkv_l, wl_l, al_l, gl_l, p)
    _, y_rl = rwkv_scan(s_ctx, r_l, vr_l, kk_l, dec_l, kd_l, bd_l, True)
    rwkv_l = rwkv_branch(y_rl, r_l, vr_l, kd_l, g_l, p, dt)

    conv_l = short_conv(ab_l, ac_l, ax_l, p['conv_a_w'])

    xl = xl + mod_l[2] * merge_branches(conv_l, rwkv_l, att_l, gate_l, p)
    xl = xl + mod_l[5] * conv_ffn(modulate(xl, p['norm2_g'], mod_l[3], mod_l[4]), p)

    if ctx_out:
        att_c = context_attention(heads_q(q_c) * ATT_SCALE, kc, vc, p['attn_sink'])
        rwkv_c = rwkv_branch(y_rc, r_c, vr_c, kd_c, g_c, p, dt)
        conv_c = short_conv(ab_c, ac_c, ax_c, p['conv_a_w'])
        xc = xc + mod_c[2] * merge_branches(conv_c, rwkv_c, att_c, gate_c, p)
        xc = xc + mod_c[5] * conv_ffn(modulate(xc, p['norm2_g'], mod_c[3], mod_c[4]), p)
    else:
        xc = None
    return xc, xl

def setup_inputs(seed: int = 0) -> dict:
    key = jax.random.key(seed)
    ks = iter(jax.random.split(key, 40))
    f = jnp.float32
    L = DEPTH

    def nrm(shape, scale):
        return jax.random.normal(next(ks), shape, f) * scale

    def gain(shape):
        return 1.0 + nrm(shape, 0.05)

    return {
        'x': nrm((BATCH, SEQ, D_MODEL), 1.0),
        'c': nrm((BATCH, D_MODEL), 1.0),
        'ctx': nrm((BATCH, CTX_LEN, D_MODEL), 1.0),
        'c_ctx': nrm((D_MODEL,), 1.0),
        'ada_w': nrm((L, D_MODEL, 6 * D_MODEL), 0.5 * D_MODEL ** -0.5),
        'ada_b': nrm((L, 6 * D_MODEL), 0.02),
        'norm1_g': gain((L, D_MODEL)),
        'w_in': nrm((L, D_MODEL, N_IN), D_MODEL ** -0.5),
        'conv_a_w': nrm((L, CONV_W, D_A), CONV_W ** -0.5),
        'a_out_w': nrm((L, D_A, D_MODEL), D_A ** -0.5),
        'rwkv_mu': jax.random.uniform(next(ks), (L, 2, 3 * D_B), f, 0.0, 0.4),
        'rwkv_w0': jax.random.uniform(next(ks), (L, 2, D_B), f, -6.0, -1.0),
        'rwkv_w2': nrm((L, 2, R_W, D_B), 0.5 * R_W ** -0.5),
        'rwkv_a0': nrm((L, 2, D_B), 0.1),
        'rwkv_a2': nrm((L, 2, R_A, D_B), R_A ** -0.5),
        'rwkv_g2': nrm((L, R_G, D_B), R_G ** -0.5),
        'rwkv_k_k': 0.85 + nrm((L, D_B), 0.05),
        'rwkv_k_a': gain((L, D_B)),
        'rwkv_r_k': nrm((L, B_HEADS, B_HEAD), 0.1),
        'rwkv_ln_g': gain((L, D_B)),
        'rwkv_ln_b': nrm((L, D_B), 0.02),
        'rwkv_out_w': nrm((L, D_B, D_MODEL), D_B ** -0.5),
        'attn_sink': nrm((L, C_HEADS), 0.5),
        'attn_out_w': nrm((L, C_HEADS * HEAD_DIM, D_MODEL), (C_HEADS * HEAD_DIM) ** -0.5),
        'w_o': nrm((L, D_MODEL, D_MODEL), D_MODEL ** -0.5),
        'norm2_g': gain((L, D_MODEL)),
        'ffn_up': nrm((L, D_MODEL, 2 * D_FF), D_MODEL ** -0.5),
        'ffn_conv': nrm((L, CONV_W, 2 * D_FF), CONV_W ** -0.5),
        'ffn_down': nrm((L, D_FF, D_MODEL), D_FF ** -0.5),
        'final_norm_g': gain((D_MODEL,)),
    }

def reference(x, c, ctx, c_ctx, ada_w, ada_b, norm1_g, w_in, conv_a_w, a_out_w, rwkv_mu, rwkv_w0, rwkv_w2,
              rwkv_a0, rwkv_a2, rwkv_g2, rwkv_k_k, rwkv_k_a, rwkv_r_k, rwkv_ln_g, rwkv_ln_b, rwkv_out_w,
              attn_sink, attn_out_w, w_o, norm2_g, ffn_up, ffn_conv, ffn_down, final_norm_g):
    cos, sin = axial_rope_tables(x.shape[1], x.dtype)
    xl, xc = x, ctx
    for i in range(DEPTH):
        p = dict(ada_w=ada_w[i], ada_b=ada_b[i], norm1_g=norm1_g[i], w_in=w_in[i], conv_a_w=conv_a_w[i],
                 a_out_w=a_out_w[i], rwkv_mu=rwkv_mu[i], rwkv_w0=rwkv_w0[i], rwkv_w2=rwkv_w2[i],
                 rwkv_a0=rwkv_a0[i], rwkv_a2=rwkv_a2[i], rwkv_g2=rwkv_g2[i], rwkv_k_k=rwkv_k_k[i],
                 rwkv_k_a=rwkv_k_a[i], rwkv_r_k=rwkv_r_k[i], rwkv_ln_g=rwkv_ln_g[i], rwkv_ln_b=rwkv_ln_b[i],
                 rwkv_out_w=rwkv_out_w[i], attn_sink=attn_sink[i], attn_out_w=attn_out_w[i], w_o=w_o[i],
                 norm2_g=norm2_g[i], ffn_up=ffn_up[i], ffn_conv=ffn_conv[i], ffn_down=ffn_down[i])
        xc, xl = trunk_layer(xc, xl, c, c_ctx, cos, sin, p, i < DEPTH - 1)
    return rmsnorm(xl, final_norm_g)


_drawn_inputs = setup_inputs


def setup_inputs(seed=0):
    import zlib

    import numpy as np

    out = dict(_drawn_inputs(seed))
    spreads = {}
    factors = {'rwkv_w2': 8.0,
     'rwkv_a0': 8.0,
     'rwkv_k_k': 4.118,
     'rwkv_k_a': 4.099,
     'rwkv_ln_g': 8.0,
     'rwkv_ln_b': 8.0,
     'attn_sink': 64.0,
     'norm2_g': 2.758}
    for name, (base, spread) in spreads.items():
        noise = np.random.default_rng([zlib.crc32(name.encode()), seed]).standard_normal(out[name].shape)
        drawn = base * np.exp(spread * noise) if base else spread * noise
        out[name] = __import__('jax').numpy.asarray(drawn.astype(out[name].dtype))
    for name, factor in factors.items():
        out[name] = (out[name] * factor).astype(out[name].dtype)
    return out
```

```python
from contextlib import ExitStack, contextmanager

import numpy as np

import concourse.bass as bass
from concourse import mybir

ALU = mybir.AluOpType
ACT = mybir.ActivationFunctionType
F32 = mybir.dt.float32
AX_X = mybir.AxisListType.X

P = 128
D = 1024
KT = D // P
SEG = 256
T = 2 * SEG
DEPTH = 2
GRID_W = 64
HEADS = 16
KV = 4
HD = 64
WINDOW = 128
D_FF = 2816
FT = D_FF // P
CH = 64
NCH = T // CH
LEVELS = 5
R_MID = 64
DECAY = float(np.exp(-0.5))
NORM_EPS = 1e-6
GN_EPS = 64e-5
KK_EPS = 1e-12
NEG = -1e30
ATT_SCALE = HD ** -0.5

COL_A = 0
COL_RKV = 3 * D
COL_W = 6 * D
COL_AL = COL_W + 2 * R_MID
COL_G = COL_AL + 2 * R_MID
COL_Q = COL_G + 128
COL_K = COL_Q + HEADS * HD
COL_V = COL_K + KV * HD
COL_GATE = COL_V + KV * HD
BURST = 2
RING = 5


def constants():
    p = np.arange(P)
    q = np.arange(P) % CH
    f = np.arange(CH)
    cols = {}
    cols["ident"] = np.eye(P)
    cols["eye64"] = (q[:, None] == f[None, :])
    cols["heads"] = (p[:, None] // HD == p[None, :] // HD)
    rot = np.zeros((P, P))
    for j in range(P):
        if j % 32 < 16:
            rot[j + 16, j] = -1.0
        else:
            rot[j - 16, j] = 1.0
    cols["rot"] = rot
    t = np.arange(SEG)
    n_freq = HD // 4
    inv = (10000.0 ** (-np.arange(n_freq, dtype=np.float32) / n_freq)).astype(np.float32)
    where = np.where((p[:, None] % HD) < 32, (t // GRID_W)[None, :], (t % GRID_W)[None, :]).astype(np.float32)
    ang = where * inv[p % n_freq][:, None]
    cols["cos"] = np.cos(ang)
    cols["sin"] = np.sin(ang)
    for name, v in (("eps_norm", NORM_EPS), ("eps_kk", KK_EPS), ("eps_gn", GN_EPS)):
        cols[name] = np.full((P, 1), v)
    for d in range(2):
        a, b = (q[:, None], f[None, :]) if d == 0 else (f[None, :], q[:, None])
        cols[f"strict{d}"] = (b > a)
        cols[f"upto{d}"] = (b >= a)
        for j in range(LEVELS + 1):
            m = 1 << j
            cols[f"level{d}{j}"] = ((a // m) % 2 == 1) & (b // m == a // m - 1)
    cols["restart"] = np.broadcast_to((np.arange(T) % CH != 0)[None, :], (P, T))
    at, made = {}, []
    for name, c in cols.items():
        n = sum(m.shape[1] for m in made)
        at[name] = (n, n + c.shape[1])
        made.append(np.asarray(c, np.float32))
    return np.concatenate(made, axis=1), at


def window_table():
    p = np.arange(P)
    k = np.arange(SEG)
    out = np.zeros((P, 2, T), np.float32)
    for b in range(2):
        out[:, b, SEG:] = np.where(np.abs(k[None, :] - (b * P + p)[:, None]) <= WINDOW, 0.0, NEG)
    return out


ORDER = ([0, 1, 2, 3, 4, 5, 6, 7], [3, 2, 1, 0, 7, 6, 5, 4])

USES = {
    ('attend', 0, 'act'): {'psum_act': 26, 'max_ready': 16},
    ('attend', 0, 'dve'): {'psum_vec': 18, 'psum_act': 26, 'head_ready': 1, 'max_ready': 16, 'exp_ready': 16,
        'prob_ready': 16, 'vec_order': 54},
    ('attend', 0, 'pe'): {'psum_act': 26, 'psum_vec': 18, 'strip': 2, 'head_ready': 1, 'prob_ready': 16},
    ('attend', 1, 'act'): {'psum_act': 14, 'max_ready': 8},
    ('attend', 1, 'dve'): {'psum_vec': 10, 'psum_act': 14, 'head_ready': 1, 'max_ready': 8, 'exp_ready': 8,
        'prob_ready': 8, 'vec_order': 30},
    ('attend', 1, 'pe'): {'psum_act': 14, 'psum_vec': 10, 'strip': 2, 'head_ready': 1, 'prob_ready': 8},
    ('merge', 0, 'act'): {'psum_act': 3, 'merged': 1},
    ('merge', 0, 'dve'): {'psum_vec': 3, 'psum_act': 3, 'merged': 1, 'vec_order': 1},
    ('merge', 0, 'pe'): {'psum_act': 3, 'psum_vec': 3, 'strip': 6},
    ('merge', 1, 'act'): {'psum_act': 3, 'merged': 1},
    ('merge', 1, 'dve'): {'psum_vec': 3, 'psum_act': 3, 'merged': 1, 'vec_order': 1},
    ('merge', 1, 'pe'): {'psum_act': 3, 'psum_vec': 3, 'strip': 6},
    ('mix', 0, 'act'): {'psum_act': 21, 'psum_dense': 7, 'cum_ready': 2, 'act_order': 1},
    ('mix', 0, 'dve'): {'psum_vec': 65, 'psum_act': 21, 'psum_dense': 7, 'kk_sq_ready': 1, 'rinv_ready': 2,
        'cum_ready': 2, 'powers_ready': 2, 'hats_ready': 2, 'v_ready': 1, 'bonus_ready': 1, 'inverse_ready': 2,
        'y_ready': 1, 'devsq_ready': 1, 'state_ready': 1, 'vec_order': 38},
    ('mix', 0, 'pe'): {'psum_act': 21, 'psum_vec': 65, 'psum_dense': 7, 'strip': 6, 'low_rank_strip': 1,
        'kk_sq_ready': 1, 'hats_ready': 2, 'v_ready': 1, 'bonus_ready': 1, 'inverse_ready': 2, 'y_ready': 1,
        'devsq_ready': 1, 'state_ready': 1},
    ('mix', 0, 'sp'): {'strip': 6, 'low_rank_strip': 1},
    ('mix', 1, 'act'): {'psum_act': 21, 'psum_dense': 7, 'cum_ready': 2, 'act_order': 1},
    ('mix', 1, 'dve'): {'psum_vec': 65, 'psum_act': 21, 'psum_dense': 7, 'kk_sq_ready': 1, 'rinv_ready': 2,
        'cum_ready': 2, 'powers_ready': 2, 'hats_ready': 2, 'v_ready': 1, 'bonus_ready': 1, 'inverse_ready': 2,
        'y_ready': 1, 'devsq_ready': 1, 'state_ready': 1, 'vec_order': 38},
    ('mix', 1, 'pe'): {'psum_act': 21, 'psum_vec': 65, 'psum_dense': 7, 'strip': 6, 'low_rank_strip': 1,
        'kk_sq_ready': 1, 'hats_ready': 2, 'v_ready': 1, 'bonus_ready': 1, 'inverse_ready': 2, 'y_ready': 1,
        'devsq_ready': 1, 'state_ready': 1},
    ('mix', 1, 'sp'): {'strip': 6, 'low_rank_strip': 1},
    ('up', 0, 'act'): {'psum_act': 4, 'up': 4, 'silu_in': 2},
    ('up', 0, 'dve'): {'psum_act': 4, 'up': 4, 'silu_in': 2, 'tanh_ready': 2, 'vec_order': 14},
    ('up', 1, 'act'): {'psum_act': 4, 'up': 4, 'silu_in': 2},
    ('up', 1, 'dve'): {'psum_act': 4, 'up': 4, 'silu_in': 2, 'tanh_ready': 2, 'vec_order': 14},
}


def uses(loop, layer, eng):
    return USES.get((loop, layer, eng), {})


class Buffers:

    def __init__(self, sem, name, n, step=1):
        self.name, self.n, self.step = name, n, step
        self.full = [sem(f"{name}_full{b}") for b in range(n)]
        self.free = [sem(f"{name}_free{b}") for b in range(n)]


class Count:

    def __init__(self, worker, name, n):
        self.name, self.n, self.at, self.used, self.term = name, n, 0, 0, 0
        self.count, self.per = [0] * n, [0] * n
        worker.counts.append(self)

    def step(self):
        b = self.at
        self.at = (b + 1) % self.n
        self.used += 1
        self.count[b] += 1
        return b, self.count[b] + self.term * self.per[b]


class Worker:

    def __init__(self, eng):
        self.eng, self.counts = eng, []

    def align(self):
        for c in self.counts:
            c.at = 0

    @contextmanager
    def loop(self, name, n, uses):
        before = [list(c.count) for c in self.counts]
        for c in self.counts:
            u = uses.get(c.name, 0)
            c.at, c.used = 0, 0
            c.per = [u // c.n + (b < u % c.n) for b in range(c.n)]
        with self.eng.Fori(0, n) as i:
            for c in self.counts:
                c.term = i
            yield i
        said = {c.name: c.used for c in self.counts if c.used}
        if said != {k: v for k, v in uses.items() if v}:
            raise ValueError(f"{name}: the body steps {said}")
        for c, b in zip(self.counts, before):
            c.count = [x + n * y for x, y in zip(b, c.per)]
            c.at, c.term, c.per = 0, 0, [0] * c.n
            c.seen = [0] * c.n


class Fill(Count):

    def __init__(self, worker, buffers):
        super().__init__(worker, buffers.name, buffers.n)
        self.b, self.seen = buffers, [0] * buffers.n

    def free(self):
        b, k = self.step()
        self.seen[b] = self.count[b]
        self.last = (b, k + 1, self.count[b] + 1)
        return self.b.free[b], k

    def full(self, token=None):
        return self.b.full[(token or self.last)[0]]

    def emptied(self, *tokens):
        newest, waits = {}, []
        for b, k, n in tokens:
            if n > newest.get(b, (0, 0))[1]:
                newest[b] = (k, n)
        for b, (k, n) in newest.items():
            if n > self.seen[b]:
                self.seen[b] = n
                waits.append((self.b.free[b], k))
        return waits


class Empty(Count):

    def __init__(self, worker, buffers):
        super().__init__(worker, buffers.name, buffers.n)
        self.b = buffers
        for b in range(buffers.n):
            worker.eng.sem_inc(buffers.free[b], 1)

    def full(self):
        b, k = self.step()
        self.last = (b, k)
        self.free = self.b.free[b]
        return self.b.full[b], k * self.b.step

    def freed(self):
        return self.free, self.last[1] + 1


class Watch(Count):

    def __init__(self, worker, buffers):
        super().__init__(worker, buffers.name, buffers.n)
        self.b = buffers

    def next(self):
        b, k = self.step()
        return self.b.free[b], k + 1

    def skip(self, n=1):
        for _ in range(n):
            self.step()


class Release(Count):

    def __init__(self, worker, buffers):
        super().__init__(worker, buffers.name, buffers.n)
        self.b = buffers
        for b in range(buffers.n):
            worker.eng.sem_inc(buffers.free[b], 1)

    def free(self):
        b, k = self.step()
        self.last = (b, k)
        return self.b.free[b]

    def freed(self):
        return self.b.free[self.last[0]], self.last[1] + 1


class Event(Count):

    def __init__(self, worker, sem, name, by=1):
        super().__init__(worker, name, 1)
        self.sem, self.by = sem, by

    def next(self):
        _, k = self.step()
        return self.sem, k * self.by


def trunk(nc, a, consts, window, x_scratch, out, at):
    ctx = ExitStack()
    with ctx:
        def sb(name, *shape):
            return ctx.enter_context(nc.sbuf_tensor(name, [P, *shape], F32))

        def sem(name):
            return ctx.enter_context(nc.semaphore(name))

        C = sb("tables", consts.shape[1])
        tab = {k: C[:, lo:hi] for k, (lo, hi) in at.items()}
        ones = sb("ones", P)
        cT = sb("cT", KT, 2)
        gh = sb("half_gate", KT, 2)
        mod = sb("mod", 6 * KT, 2)
        gs = sb("gain_scale", KT, 2)
        rows = sb("param_rows", 4, P)
        pp = sb("params", 24, KT)
        pb = sb("params_b", 88)
        pf = sb("params_ffn", 3 * 2 * FT)
        sink = sb("sink", DEPTH, HEADS)
        pc = sb("params_pair", 27)
        pa = sb("params_pair_act", 4)
        pg = sb("params_norm", 2)
        strip = sb("strips", RING, KT, P)
        lw = sb("low_rank_out", 3, P)
        hT = sb("hT", KT, T)
        yA = sb("conv_branch", KT, T)
        yB = sb("rwkv_branch", KT, T)
        low = sb("low_rank", 3, T)
        ARENA = 29728
        arena = sb("arena", ARENA)

        class Region:
            def __init__(self):
                self.at = 0

            def __call__(self, *shape):
                n = int(np.prod(shape))
                assert self.at + n <= ARENA, (self.at, n)
                v = arena[:, self.at:self.at + n]
                self.at += n
                if len(shape) == 2:
                    v = v.rearrange("p (a b) -> p a b", a=shape[0])
                elif len(shape) == 3:
                    v = v.rearrange("p (a b c) -> p a b c", a=shape[0], b=shape[1])
                return v

        ra = Region()
        AR = [ra(3, T) for _ in range(2)]
        LB = [ra(NCH, 3, CH) for _ in range(2)]
        MK = [ra(NCH, 2, CH) for _ in range(2)]
        KM = [ra(NCH, CH) for _ in range(2)]
        TT = [ra(NCH, CH) for _ in range(2)]
        ZZ = [ra(NCH, CH) for _ in range(2)]
        XX = [ra(NCH, CH) for _ in range(2)]
        AM = [ra(NCH, 2, CH) for _ in range(2)]
        WU = [ra(NCH, 2, CH) for _ in range(2)]
        BT = [WU[d][:, 0:4].rearrange("p c j t -> p (c j t)") for d in range(2)]
        KTr = [WU[d][:, 4:8].rearrange("p c j t -> p (c j t)") for d in range(2)]
        GG, CC = TT, XX
        VM = ra(NCH, CH)
        rkvp = ra(3, 2, SEG + 2)
        rkv = ra(3, T)
        th = ra(4, T)
        cum = ra(T)
        Pe, Pi, Pn = ra(T), ra(T), ra(T)
        kk = ra(T)
        t1, t2 = ra(T), ra(T)
        kd = ra(2, T)
        bon = ra(T)
        gb = ra(T)
        acb = ra(T)
        axp = ra(2, SEG + 2)
        cvt = ra(T)
        PC = ra(2, NCH)
        ysum = ra(T)
        rinv = cvt

        rx = Region()
        xT = rx(KT, T)
        mark = rx.at
        yC = rx(KT, T)
        after_y = rx.at
        K2 = rx(KV, T)
        K1 = rx(2, T)
        VT = rx(4, KV * HD)
        kcur, vcur = rx(T), rx(4, HD)
        win = rx(2, T)
        qs = rx(2, T)
        rot_t, cos_t = rx(SEG), rx(SEG)
        sc = rx(2, T)
        pr = rx(2, T)
        pT = rx(4, SEG)
        st = rx(64)
        sinkc = rx(4)
        rx.at = after_y
        mT = rx(KT, T)
        sg = rx(3, T)
        mt = rx(2, T)
        rx.at = mark
        hid = rx(FT, T)
        upp = rx(4, 2, SEG + 2)
        upc = rx(2, T)
        upt = rx(2, T)
        pfc = rx(2, 6)
        rx.at = mark
        sq = rx(KT, T)
        rs = rx(T)
        rx.at = mark
        unit = rx(2, KT, 512)
        xin = rx(4, D)
        crow = rx(P)
        ct = rx(2 * KT)
        rx.at = mark
        yout = rx(2, D)

        PS = ctx.enter_context(nc.psum_tensor("psum", [P, 8, 512], F32))
        BANK_A = [0, 1]
        BANK_G = [6, 7]
        BANK_D = [2, 3, 4, 5]
        forA = Buffers(sem, "psum_act", 2)
        forG = Buffers(sem, "psum_dense", 2)
        forD = Buffers(sem, "psum_vec", 4)
        ring = Buffers(sem, "strip", RING, 16)
        lowr = Buffers(sem, "low_rank_strip", 1, 48)
        adab = Buffers(sem, "ada_unit", 2, 16)

        s_gate = sem("gate")
        s_phase = sem("phase_done")
        s_load = sem("loads")
        s_vec, s_act = sem("vec_order"), sem("act_order")
        s_tab = sem("tables_loaded")
        up_buf = Buffers(sem, "up", 4)
        ev = {n: sem(n) for n in (
            "kk_sq_ready", "rinv_ready", "cum_ready", "powers_ready", "hats_ready", "v_ready", "bonus_ready",
            "inverse_ready", "y_ready", "devsq_ready", "state_ready", "sq_ready", "rs_ready", "head_ready",
            "max_ready", "exp_ready", "prob_ready", "silu_in", "tanh_ready", "merged", "unit_fill")}

        engines = 4
        block = ctx.enter_context(nc.Block())

        class Phases:

            def __init__(self, eng):
                self.eng, self.n = eng, 0

            def __call__(self):
                self.n += engines
                self.eng.drain().then_inc(s_phase, 1)
                self.eng.wait_ge(s_phase, self.n)

        def wcols(w, col, nk=KT, k0=0, n=P):
            return w[k0 * P:(k0 + nk) * P, bass.ds(col, n)].rearrange("(k p) n -> p k n", p=P)


        @block.sync
        def _(sp):
            w = Worker(sp)
            rg = Fill(w, ring)
            lr = Fill(w, lowr)
            au = Fill(w, adab)

            def load(src, nk=KT):
                sp.wait_ge(*rg.free())
                sp.sem_inc(s_gate, 1)
                b = rg.last[0]
                sp.dma_start(strip[:, b, 0:nk, :], src).then_inc(rg.full(), 16)

            sp.dma_start(C[:, :], consts).then_inc(s_tab, 16)
            for l in range(DEPTH):
                wi = a["w_in"][l]
                sp.wait_ge(ev["unit_fill"], l + 1)
                with w.loop("ada", 6, {"ada_unit": 2}) as i:
                    for j in range(2):
                        sp.wait_ge(*au.free())
                        sp.sem_inc(s_gate, 1)
                        b = au.last[0]
                        sp.dma_start(unit[:, b], wcols(a["ada_w"][l], i * 1024 + j * 512, n=512))\
                            .then_inc(au.full(), 16)
                for c in (COL_W, COL_AL, COL_G):
                    load(wcols(wi, c))
                with w.loop("mix", KT, uses("mix", l, "sp")) as i:
                    for q in range(2):
                        load(wcols(wi, i * P + COL_RKV + q * D))
                    sp.wait_ge(*lr.free())
                    sp.sem_inc(s_gate, 1)
                    cols = bass.ds(i * P, P)
                    sp.dma_start(lw[:, 0, :], a["rwkv_w2"][l].rearrange("d r c -> (d r) c")[:, cols])\
                        .then_inc(lr.full(), 16)
                    sp.dma_start(lw[:, 1, :], a["rwkv_a2"][l].rearrange("d r c -> (d r) c")[:, cols])\
                        .then_inc(lr.full(), 16)
                    sp.dma_start(lw[:, 2, :], a["rwkv_g2"][l][:, cols]).then_inc(lr.full(), 16)
                    for col in (D, 2 * D, 0, COL_RKV + 2 * D):
                        load(wcols(wi, i * P + col))
                for c in range(4):
                    load(wcols(wi, COL_K + c * P))
                with w.loop("attend", KV, {"strip": 2}) as i:
                    for u in range(2):
                        load(wcols(wi, i * 2 * P + COL_Q + u * P))
                with w.loop("merge", KT, {"strip": 6}) as i:
                    for q, y in enumerate(("a_out_w", "rwkv_out_w", "attn_out_w")):
                        load(wcols(wi, i * P + COL_GATE + q * D))
                        load(wcols(a[y][l], i * P))
                with w.loop("w_o", KT // 4, {"strip": 4}) as i:
                    for j in range(4):
                        load(wcols(a["w_o"][l], i * 4 * P + j * P))
                with w.loop("up", FT // 2, {"strip": 4}) as i:
                    for j in range(2):
                        load(wcols(a["ffn_up"][l], i * 2 * P + j * P))
                        load(wcols(a["ffn_up"][l], i * 2 * P + j * P + D_FF))
                with w.loop("down", KT, {"strip": 3}) as i:
                    for k0, nk in ((0, 8), (8, 8), (16, 6)):
                        load(wcols(a["ffn_down"][l], i * P, nk, k0), nk)

        @block.gpsimd
        def _(pool):
            w = Worker(pool)
            loads = Event(w, s_load, "loads", 16)
            phase = Phases(pool)

            def move(dst, src):
                loads.step()
                pool.dma_start(dst, src).then_inc(s_load, 16)

            def settle():
                pool.wait_ge(s_load, loads.count[0] * 16)

            for l in range(DEPTH):

                def turn(name):
                    v = a[name][l]
                    if len(v.shape) == 2:
                        v = v.rearrange("a b -> (a b)")
                    return v.rearrange("(g p) -> g p", p=P)

                r = 0
                for name in ("rwkv_mu", "rwkv_w0", "rwkv_a0", "rwkv_k_k", "rwkv_k_a", "rwkv_r_k",
                             "rwkv_ln_g", "rwkv_ln_b", "norm1_g"):
                    v = turn(name)
                    move(rows[r:r + v.shape[0], 0, :], v)
                    r += v.shape[0]
                r = 0
                for name in ("conv_a_w", "norm2_g", "ada_b"):
                    v = turn(name)
                    move(rows[r:r + v.shape[0], 1, :], v)
                    r += v.shape[0]
                move(rows[r:r + KT, 1, :], a["final_norm_g"].rearrange("(g p) -> g p", p=P))
                v = turn("ffn_conv")
                move(rows[:, 2, :], v[0:P])
                move(rows[0:4, 3, :], v[P:P + 4])
                if l == 0:
                    pool.memset(ones[:, :], 1.0)
                    move(crow[0:KT, :], a["c"].rearrange("b (g p) -> (b g) p", p=P))
                    move(crow[KT:2 * KT, :], a["c_ctx"].rearrange("(g p) -> g p", p=P))
                    for j in range(2):
                        move(xin[:, j, :], a["ctx"][0, j * P:(j + 1) * P, :])
                        move(xin[:, 2 + j, :], a["x"][0, j * P:(j + 1) * P, :])
                    for m in range(DEPTH):
                        move(sink[:, m, :], a["attn_sink"][m].partition_broadcast(P))
                settle()
                pool.drain().then_inc(ev["unit_fill"], 1)
                phase()
                phase()
                phase()
                phase()
                move(x_scratch, xT.rearrange("p k t -> p (k t)"))
                settle()
                phase()
                phase()
                move(win.rearrange("p b t -> p (b t)"), window)
                settle()
                phase()
                move(xT.rearrange("p k t -> p (k t)"), x_scratch)
                settle()
                for j in range(KV):
                    src = K1[64 * (j % 2):64 * (j % 2) + 64, j // 2, :]
                    move(K2[0:64, j, :], src)
                    move(K2[64:128, j, :], src)
                settle()
                phase()
                phase()
                phase()
                phase()
                phase()
                phase()
                phase()
            phase()
            for j in range(2):
                move(out[0, j * P:(j + 1) * P, :], yout[:, j, :])
            settle()

        @block.tensor
        def _(pe):
            w = Worker(pe)
            A, Dv, G = Fill(w, forA), Fill(w, forD), Fill(w, forG)
            rg = Empty(w, ring)
            lr = Empty(w, lowr)
            au = Empty(w, adab)
            E = {n: Event(w, ev[n], n) for n in ("kk_sq_ready", "hats_ready", "v_ready", "bonus_ready",
                                                 "inverse_ready", "y_ready", "devsq_ready", "state_ready",
                                                 "sq_ready", "head_ready", "prob_ready")}
            phase = Phases(pe)
            owed = [None]

            def go():
                pe.sem_inc(s_gate, 1)

            def bank(F):
                return PS[:, (BANK_G if F is G else BANK_A if F is A else BANK_D)[F.last[0]], :]

            def mm(o, lhs, rhs, start=True, stop=True):
                ins = pe.matmul(o, lhs, rhs, start=start, stop=stop)
                return ins

            def flush():
                if owed[0] is not None:
                    pe.drain().then_inc(owed[0], 1)
                    owed[0] = None

            def product(F, lo, rhs, parts=(KT,)):
                pe.wait_ge(*F.free())
                o = bank(F)[:, lo:T]
                n, k = sum(parts), 0
                for nk in parts:
                    pe.wait_ge(*rg.full())
                    s = rg.last[0]
                    for j in range(nk):
                        ins = mm(o, strip[:, s, j, :], rhs(k), k == 0, k == n - 1)
                        if j == 0 and owed[0] is not None:
                            ins.then_inc(owed[0], 1)
                            owed[0] = None
                        k += 1
                    if k < n:
                        ins.then_inc(rg.free, 1)
                    else:
                        owed[0] = rg.free
                ins.then_inc(F.full(), 1)
                return F.last

            pe.wait_ge(s_tab, 16)

            def norm_sum(lo):
                pe.wait_ge(*A.free())
                o = bank(A)
                for k in range(KT):
                    pe.wait_ge(*E["sq_ready"].next())
                    ins = mm(o[:, lo:T], ones[:, :], sq[:, k, lo:T], k == 0, k == KT - 1)
                ins.then_inc(A.full(), 1)

            def setup(l):
                for j, n in enumerate((P, 88, P, 4)):
                    pe.wait_ge(*Dv.free())
                    o = bank(Dv)
                    ins = pe.transpose(o[:, 0:n], rows[0:n, j, :], tab["ident"][0:n, 0:n])
                    ins.then_inc(Dv.full(), 1)
                if l == 0:
                    pe.wait_ge(*Dv.free())
                    o = bank(Dv)
                    pe.transpose(o[:, 0:2 * KT], crow[0:2 * KT, :], tab["ident"][0:2 * KT, 0:2 * KT]).then_inc(Dv.full(), 1)
                    for k in range(KT):
                        pe.wait_ge(*Dv.free())
                        o = bank(Dv)
                        for j in range(4):
                            ins = pe.transpose(o[:, j * P:(j + 1) * P], xin[:, j, k * P:(k + 1) * P],
                                               tab["ident"])
                        ins.then_inc(Dv.full(), 1)

            def ada():
                with w.loop("ada", 6, {"ada_unit": 2, "psum_vec": 2}) as i:
                    for _ in range(2):
                        pe.wait_ge(*au.full())
                        u = au.last[0]
                        pe.wait_ge(*Dv.free())
                        o = bank(Dv)
                        for m in range(4):
                            for k in range(KT):
                                ins = mm(o[:, 2 * m:2 * m + 2], unit[:, u, k, m * P:(m + 1) * P], cT[:, k, :],
                                         k == 0, k == KT - 1)
                        ins.then_inc(Dv.full(), 1)
                        pe.drain().then_inc(au.free, 1)

            def mix(l, lo):
                n_y = (T - lo) // CH
                c0 = lo // CH
                def strip_tiles(first):
                    pe.wait_ge(*G.free())
                    pe.wait_ge(*rg.full())
                    o, b = bank(G), rg.last[0]
                    for k in range(KT):
                        ins = mm(o[:, first:T], strip[:, b, k, :], hT[:, k, first:T], k == 0, k == KT - 1)
                        if k == 0 and owed[0] is not None:
                            ins.then_inc(owed[0], 1)
                            owed[0] = None
                        if k == KT - 1:
                            ins.then_inc(G.full(), 1)
                            owed[0] = rg.free
                        yield

                def decay_product(j):
                    if j == 0:
                        pe.wait_ge(*lr.full())
                    q, d = j // 2, j % 2
                    pe.wait_ge(*A.free())
                    o = bank(A)
                    mm(o, lw[64 * d:64 * d + 64, q, :], low[64 * d:64 * d + 64, q, :]).then_inc(A.full(), 1)

                def dense_products():
                    yield from strip_tiles(0)
                    yield from strip_tiles(0)
                    yield from strip_tiles(lo)
                    yield from strip_tiles(lo)
                    pe.wait_ge(*E["kk_sq_ready"].next())
                    pe.wait_ge(*G.free())
                    o = bank(G)
                    mm(o, tab["heads"], t1).then_inc(G.full(), 1)
                    yield
                    yield from strip_tiles(lo)
                    yield from strip_tiles(0)

                def chunks(ahead):
                    steps = dense_products() if ahead else iter(())

                    due = [0]

                    def dense(n=1, burst=BURST):
                        due[0] += n
                        if due[0] >= burst:
                            for _ in range(due[0]):
                                next(steps, None)
                            due[0] = 0

                    pe.wait_ge(*A.free())
                    o = bank(A)
                    mm(o[:, lo:T], lw[:, 2, :], low[:, 2, lo:T]).then_inc(A.full(), 1)
                    pe.drain().then_inc(lr.free, 1)
                    pe.wait_ge(*E["v_ready"].next())
                    pe.wait_ge(*A.free())
                    o = bank(A)
                    for cp in range(4):
                        ins = pe.transpose(o[:, cp * P:(cp + 1) * P], rkv[:, 2, cp * P:(cp + 1) * P], tab["ident"])
                    ins.then_inc(A.full(), 1)
                    t_v = A.last
                    dense(KT)
                    HP = ((0, 0), (1, 1), (0, 1), (1, 0))
                    t_lr, t_mk, t_l, t_tr = [], [], [], []
                    for d in range(2):
                        pe.wait_ge(*E["hats_ready"].next())
                        for left, wide, toks in ((BT, 2, t_lr), (KTr, 2, t_mk), (None, 1, t_l)):
                            pe.wait_ge(*Dv.free())
                            first, outs = Dv.last, [bank(Dv)]
                            pe.wait_ge(*Dv.free())
                            second = Dv.last
                            outs.append(bank(Dv))
                            go()
                            for cp in range(4):
                                for h, p in HP:
                                    c, r = 2 * cp + p, slice(64 * h, 64 * h + 64)
                                    o = outs[h][64 * p:64 * p + 64, cp * wide * CH:(cp + 1) * wide * CH]
                                    if left is not None:
                                        lhs = left[d][r, c * CH:(c + 1) * CH]
                                        rhs = AR[d][r, 0:2, c * CH:(c + 1) * CH]
                                        o = o.rearrange("p (j t) -> p j t", j=2)
                                    else:
                                        lhs, rhs = AR[d][r, 0, c * CH:(c + 1) * CH], BT[d][r, c * CH:(c + 1) * CH]
                                    ins = mm(o, lhs, rhs)
                                    if cp == 3 and (h, p) == (0, 1):
                                        ins.then_inc(Dv.full(first), 1)
                            ins.then_inc(Dv.full(second), 1)
                            toks.append((first, second))
                            dense()
                        for src in (AR, BT, KTr):
                            pe.wait_ge(*A.free())
                            o = bank(A)
                            for cp in range(4):
                                v = (src[d][:, 0] if src is AR else src[d])[:, cp * P:(cp + 1) * P]
                                ins = pe.transpose(o[:, cp * P:(cp + 1) * P], v, tab["ident"])
                            ins.then_inc(A.full(), 1)
                            t_tr.append(A.last)
                        dense()

                    pe.wait_ge(*E["bonus_ready"].next())
                    pe.wait_ge(*Dv.free())
                    o = bank(Dv)
                    mm(o[:, lo:T], tab["heads"], t2[:, lo:T]).then_inc(Dv.full(), 1)

                    def each(o, lhs, rhs, n=CH, cols=None):
                        for q in range(NCH):
                            for p in range(2):
                                r = slice(64 * p, 64 * p + 64)
                                ins = mm(o[r, q * n:(q + 1) * n], lhs[r, q], rhs[r, q])
                        return ins

                    t_mv = []
                    for d in range(2):
                        pe.wait_ge(*A.free())
                        o = bank(A)
                        for w_emptied in A.emptied(t_v):
                            pe.wait_ge(*w_emptied)
                        for w_emptied in Dv.emptied(*t_mk[d]):
                            pe.wait_ge(*w_emptied)
                        go()
                        ins = each(o, MK[d][:, :, 0, :], VM)
                        ins.then_inc(A.full(), 1)
                        t_mv.append(A.last)
                        if ahead:
                            decay_product(d)
                    t_z, t_t = [None, None], [None, None]
                    for j in range(LEVELS):
                        t_x = []
                        for d in range(2):
                            pe.wait_ge(*Dv.free())
                            o = bank(Dv)
                            if t_z[d]:
                                for w_emptied in Dv.emptied(t_t[d], t_z[d]):
                                    pe.wait_ge(*w_emptied)
                            else:
                                pe.wait_ge(*E["inverse_ready"].next())
                            go()
                            each(o, LB[d][:, :, 0, :], TT[d]).then_inc(Dv.full(), 1)
                            t_x.append(Dv.last)
                            if ahead and j == 0:
                                decay_product(2 + d)
                            dense()
                        for d in range(2):
                            pe.wait_ge(*Dv.free())
                            o = bank(Dv)
                            for w_emptied in Dv.emptied(t_x[d]):
                                pe.wait_ge(*w_emptied)
                            go()
                            if j < LEVELS - 1:
                                each(o, ZZ[d], XX[d]).then_inc(Dv.full(), 1)
                                t_t[d] = Dv.last
                                dense()
                                pe.wait_ge(*Dv.free())
                                o = bank(Dv)
                                go()
                            each(o, XX[d], ZZ[d]).then_inc(Dv.full(), 1)
                            t_z[d] = Dv.last
                            if j < LEVELS - 1 or d == 0:
                                dense()
                    dense(0, 0)
                    t_wu = []
                    for d in range(2):
                        for half in range(2):
                            pe.wait_ge(*A.free())
                            o = bank(A)
                            for w_emptied in A.emptied(*t_mv, *t_tr):
                                pe.wait_ge(*w_emptied)
                            for w_emptied in Dv.emptied(t_z[d]):
                                pe.wait_ge(*w_emptied)
                            go()
                            for q in range(4 * half, 4 * half + 4):
                                for p in range(2):
                                    r = slice(64 * p, 64 * p + 64)
                                    ins = mm(o[r, (q % 4) * P:(q % 4 + 1) * P], ZZ[d][r, q],
                                             AM[d][r, q].rearrange("p j t -> p (j t)"))
                            ins.then_inc(A.full(), 1)
                            t_wu.append(A.last)
                    for d in range(2):
                        for w_emptied in A.emptied(*t_wu[2 * d:2 * d + 2]):
                            pe.wait_ge(*w_emptied)
                        for kind in range(2):
                            pe.wait_ge(*Dv.free())
                            first, outs = Dv.last, [bank(Dv)]
                            pe.wait_ge(*Dv.free())
                            second = Dv.last
                            outs.append(bank(Dv))
                            go()
                            for cp in range(4):
                                for h, p in HP:
                                    q, r = 4 * h + cp, slice(64 * p, 64 * p + 64)
                                    if kind == 0:
                                        o = outs[p][64 * h:64 * h + 64, cp * P:(cp + 1) * P]
                                        ins = mm(o, WU[d][r, q, 0, :],
                                                 LB[d][r, q, 1:3, :].rearrange("p j t -> p (j t)"))
                                    else:
                                        o = outs[p][64 * h:64 * h + 64, cp * CH:(cp + 1) * CH]
                                        mm(o, LB[d][r, q, 2, :], WU[d][r, q, 1, :], True, False)
                                        ins = mm(o, KM[d][r, q, :], VM[r, q, :], False, True)
                                    if cp == 3 and (h, p) == (1, 0):
                                        last0 = ins
                                    if cp == 3 and (h, p) == (0, 1):
                                        last1 = ins
                            last0.then_inc(Dv.full(first), 1)
                            last1.then_inc(Dv.full(second), 1)
                    pe.wait_ge(*A.free())
                    first, outs = A.last, [bank(A)]
                    pe.wait_ge(*A.free())
                    second = A.last
                    outs.append(bank(A))
                    go()
                    last = [None, None]
                    for c in range(c0, NCH):
                        cp, p = c // 2, c % 2
                        for h in range(2):
                            q, r = 4 * h + cp, slice(64 * p, 64 * p + 64)
                            o = outs[p][64 * h:64 * h + 64, cp * CH:(cp + 1) * CH]
                            for d in range(2):
                                mm(o, WU[d][r, q, 1, :], LB[d][r, q, 1, :], d == 0, False)
                                ins = mm(o, VM[r, q, :], MK[d][r, q, 1, :], False, d == 1)
                            last[p] = ins
                    last[0].then_inc(A.full(first), 1)
                    last[1].then_inc(A.full(second), 1)
                    pe.wait_ge(*E["state_ready"].next())
                    t_s = [None, None]
                    for s in range(NCH - 1):
                        for d in range(2):
                            c = ORDER[d][s]
                            pe.wait_ge(*Dv.free())
                            o = bank(Dv)
                            if t_s[d]:
                                for w_emptied in Dv.emptied(t_s[d]):
                                    pe.wait_ge(*w_emptied)
                            go()
                            for h in range(2):
                                r = slice(64 * h, 64 * h + 64)
                                ins = mm(o[r, 0:CH], AR[d][r, 2, c * CH:(c + 1) * CH], GG[d][r, c, :])
                            ins.then_inc(Dv.full(), 1)
                            t_s[d] = Dv.last
                        dense()
                    dense(2, 0)
                    pe.wait_ge(*Dv.free())
                    o = bank(Dv)
                    for w_emptied in Dv.emptied(*t_s):
                        pe.wait_ge(*w_emptied)
                    go()
                    for c in range(c0, NCH):
                        for d in range(2):
                            for h in range(2):
                                r = slice(64 * h, 64 * h + 64)
                                ins = mm(o[r, c * CH:(c + 1) * CH], GG[d][r, c, :], AR[d][r, 1, c * CH:(c + 1) * CH],
                                         d == 0, d == 1)
                    ins.then_inc(Dv.full(), 1)
                    flush()
                    assert next(steps, None) is None
                    pe.wait_ge(*E["y_ready"].next())
                    pe.wait_ge(*Dv.free())
                    o = bank(Dv)
                    mm(o[:, lo:T], tab["heads"], ysum[:, lo:T]).then_inc(Dv.full(), 1)
                    pe.wait_ge(*E["devsq_ready"].next())
                    pe.wait_ge(*A.free())
                    o = bank(A)
                    mm(o[:, lo:T], tab["heads"], t1[:, lo:T]).then_inc(A.full(), 1)

                w.align()
                for _ in dense_products():
                    pass
                for j in range(4):
                    decay_product(j)
                flush()
                with w.loop("mix", KT - 1, uses("mix", l, "pe")):
                    chunks(True)
                chunks(False)

            def keys_values():
                t_k = [product(A, 0, lambda k: hT[:, k, :]) for q in range(2)]
                for q in range(2):
                    pe.wait_ge(*rg.full())
                    s = rg.last[0]
                    pe.wait_ge(*A.free())
                    o = bank(A)
                    for j in range(4):
                        for k in range(KT):
                            ins = mm(o[:, j * P:(j + 1) * P], hT[:, k, j * P:(j + 1) * P], strip[:, s, k, :],
                                     k == 0, k == KT - 1)
                            if j == 0 and k == 0 and owed[0] is not None:
                                ins.then_inc(owed[0], 1)
                                owed[0] = None
                    ins.then_inc(A.full(), 1)
                    owed[0] = rg.free
                for q in range(2):
                    for w_emptied in A.emptied(t_k[q]):
                        pe.wait_ge(*w_emptied)
                    pe.wait_ge(*Dv.free())
                    o = bank(Dv)
                    mm(o[:, 0:SEG], tab["rot"], K1[:, q, SEG:T]).then_inc(Dv.full(), 1)
                flush()

            def attend(l, lo):
                tiles = [j for j in range(4) if j * P >= lo]
                with w.loop("attend", KV, uses("attend", l, "pe")) as i:
                    t_q = []
                    for u in range(2):
                        t_q.append(product(A, lo, lambda k: hT[:, k, lo:T]))
                    for u in range(2):
                        for w_emptied in A.emptied(t_q[u]):
                            pe.wait_ge(*w_emptied)
                        pe.wait_ge(*Dv.free())
                        o = bank(Dv)
                        mm(o[:, 0:SEG], tab["rot"], qs[:, u, SEG:T]).then_inc(Dv.full(), 1)
                    flush()
                    pe.wait_ge(*E["head_ready"].next())
                    for u in range(2):
                        for hh in range(2):
                            r = slice(64 * hh, 64 * hh + 64)
                            for seg in range(lo // SEG, 2):
                                nk = SEG if seg == 0 else T
                                for j in range(2):
                                    pe.wait_ge(*Dv.free())
                                    o = bank(Dv)
                                    mm(o[:, 0:nk], qs[r, u, seg * SEG + j * P:seg * SEG + (j + 1) * P],
                                                kcur[r, 0:nk]).then_inc(Dv.full(), 1)
                                for j in range(2):
                                    pe.wait_ge(*E["prob_ready"].next())
                                    pe.wait_ge(*A.free())
                                    o = bank(A)
                                    for k in range(nk // P):
                                        ins = pe.transpose(o[:, k * P:(k + 1) * P], pr[:, j, k * P:(k + 1) * P],
                                                           tab["ident"])
                                    ins.then_inc(A.full(), 1)
                                    t_p = A.last
                                for w_emptied in A.emptied(t_p):
                                    pe.wait_ge(*w_emptied)
                                pe.wait_ge(*A.free())
                                o = bank(A)
                                for k in range(nk // P):
                                    ins = mm(o[r, 0:SEG], vcur[:, k, :], pT[:, k, :], k == 0, k == nk // P - 1)
                                ins.then_inc(A.full(), 1)

            def merge(l, lo):
                with w.loop("merge", KT, uses("merge", l, "pe")) as i:
                    for y in (yA, yB, yC):
                        product(A, lo, lambda k: hT[:, k, lo:T])
                        product(Dv, lo, lambda k: y[:, k, lo:T])
                    flush()
                phase()
                with w.loop("w_o", KT // 4, {"strip": 4, "psum_vec": 4}) as i:
                    for j in range(4):
                        product(Dv, lo, lambda k: mT[:, k, lo:T])
                    flush()
                phase()

            def ffn(l, lo):
                with w.loop("up", FT // 2, {"strip": 4, "psum_act": 4}) as i:
                    for j in range(4):
                        product(A, lo, lambda k: hT[:, k, lo:T])
                    flush()
                phase()
                with w.loop("down", KT, {"strip": 3, "psum_vec": 1}) as i:
                    product(Dv, lo, lambda k: hid[:, k, lo:T], (8, 8, 6))
                    flush()
                phase()

            for l in range(DEPTH):
                lo = 0 if l < DEPTH - 1 else SEG
                phase()
                setup(l)
                phase()
                ada()
                phase()
                norm_sum(0)
                phase()
                for j in range(3):
                    product(A, 0, lambda k: hT[:, k, :])
                flush()
                phase()
                mix(l, lo)
                phase()
                keys_values()
                phase()
                phase()
                attend(l, lo)
                phase()
                merge(l, lo)
                norm_sum(lo)
                phase()
                ffn(l, lo)
            norm_sum(SEG)
            for j in range(2):
                for half in range(2):
                    if j == 0 and half == 0:
                        pe.wait_ge(*E["y_ready"].next())
                    pe.wait_ge(*Dv.free())
                    o = bank(Dv)
                    for k in range(4):
                        ins = pe.transpose(o[:, k * P:(k + 1) * P],
                                           hT[:, 4 * half + k, SEG + j * P:SEG + (j + 1) * P], tab["ident"])
                    ins.then_inc(Dv.full(), 1)
            phase()

        @block.scalar
        def _(act):
            w = Worker(act)
            A, G = Empty(w, forA), Empty(w, forG)
            uf = Fill(w, up_buf)
            E = {n: Event(w, ev[n], n) for n in ("cum_ready", "max_ready", "silu_in", "merged")}
            order = Event(w, s_act, "act_order")
            phase = Phases(act)
            act.wait_ge(s_tab, 16)

            def A_bank():
                return PS[:, BANK_A[A.last[0]], :]

            def copy(o, i):
                return act.copy(o, i)

            def rsqrt(dst, src, scale, eps):
                act.activation(dst, src, ACT.Ln, bias=eps, scale=scale).then_inc(A.free, 1)
                act.wait_ge(*A.freed())
                return act.activation(dst, dst, ACT.Exp, scale=-0.5)

            def norm(lo):
                act.wait_ge(*A.full())
                o = A_bank()
                rsqrt(rs[:, lo:T], o[:, lo:T], 1.0 / D, tab["eps_norm"]).then_inc(ev["rs_ready"], 1)

            def mix(l, lo):
                s0 = lo // SEG
                c0 = lo // P
                def G_bank():
                    return PS[:, BANK_G[G.last[0]], :]

                def shifted(q):
                    act.wait_ge(*G.full())
                    act.copy(rkvp[:, q, :, 1:SEG + 1], G_bank().rearrange("p (s t) -> p s t", s=2)).then_inc(G.free, 1)

                def bias_of(i):
                    act.copy(pa[:, :].unsqueeze(2), pp[:, 19:23, bass.ds(i, 1)]).then_inc(s_act, 1)
                    act.wait_ge(*order.next())

                def decay(j):
                    act.wait_ge(*A.full())
                    o = A_bank()
                    act.activation(th[:, j, :], o, ACT.Tanh, bias=pa[:, j:j + 1], scale=0.5).then_inc(A.free, 1)

                def conv_inputs():
                    act.wait_ge(*G.full())
                    act.copy(acb[:, lo:T], G_bank()[:, lo:T]).then_inc(G.free, 1)
                    act.wait_ge(*G.full())
                    act.copy(axp[:, s0:, 1:SEG + 1], G_bank()[:, lo:T].rearrange("p (s t) -> p s t", t=SEG)).then_inc(G.free, 1)

                def key_norm():
                    act.wait_ge(*G.full())
                    act.activation(rinv[:, :], G_bank(), ACT.Ln, bias=tab["eps_kk"]).then_inc(G.free, 1)
                    act.wait_ge(*G.freed())
                    act.activation(rinv[:, :], rinv[:, :], ACT.Exp, scale=-0.5).then_inc(ev["rinv_ready"], 1)

                def conv_gate(i):
                    act.wait_ge(*G.full())
                    act.copy(yA[:, bass.ds(i, 1), lo:T], G_bank()[:, lo:T].unsqueeze(1)).then_inc(G.free, 1)

                def powers(d):
                    act.wait_ge(*E["cum_ready"].next())
                    act.activation(Pe[:, :], t1[:, :], ACT.Exp)
                    act.activation(Pi[:, :], cum[:, :], ACT.Exp)
                    act.activation(Pn[:, :], cum[:, :], ACT.Exp, scale=-1.0)
                    end = CH - 1 if d == 0 else 0
                    act.activation(PC[:, d, :], cum[:, end:T:CH], ACT.Exp).then_inc(ev["powers_ready"], 1)

                def by_problem(v):
                    return v.rearrange("p (c h t) -> p h c t", c=4, h=2)

                def problems(v):
                    return v.rearrange("p (h c) t -> p h c t", h=2)

                def chunks(i, ahead):
                    powers(0)
                    act.wait_ge(*A.full())
                    o = A_bank()
                    act.copy(gb[:, lo:T], o[:, lo:T]).then_inc(A.free, 1)
                    act.wait_ge(*A.full())
                    o = A_bank()
                    act.copy(problems(VM), by_problem(o)).then_inc(A.free, 1)
                    if ahead:
                        shifted(0)
                    powers(1)
                    for d in range(2):
                        for dst in (AM[d][:, :, 0, :], LB[d][:, :, 2, :], KM[d]):
                            act.wait_ge(*A.full())
                            o = A_bank()
                            act.copy(problems(dst), by_problem(o)).then_inc(A.free, 1)
                    if ahead:
                        bias_of(i + 1)
                    for d in range(2):
                        act.wait_ge(*A.full())
                        o = A_bank()
                        act.copy(AM[d][:, :, 1, :], o.rearrange("p (q t) -> p q t", q=NCH)).then_inc(A.free, 1)
                        if ahead:
                            decay(d)
                    if ahead:
                        decay(2)
                        decay(3)
                        shifted(1)
                        conv_inputs()
                        key_norm()
                        conv_gate(i + 1)
                    for d in range(2):
                        for half in range(2):
                            act.wait_ge(*A.full())
                            o = A_bank()
                            act.copy(WU[d][:, 4 * half:4 * half + 4].rearrange("p q j t -> p (q j t)"), o).then_inc(A.free, 1)
                    for p in range(2):
                        act.wait_ge(*A.full())
                        o = A_bank()
                        act.copy(ysum.rearrange("p (c q t) -> p c q t", c=4, q=2)[:, c0:, p, :],
                                 o[:, c0 * CH:4 * CH].rearrange("p (c t) -> p c t", t=CH)).then_inc(A.free, 1)
                    if ahead:
                        shifted(2)
                    act.wait_ge(*A.full())
                    o = A_bank()
                    rsqrt(rinv[:, lo:T], o[:, lo:T], 1.0 / HD, tab["eps_gn"]).then_inc(ev["rinv_ready"], 1)

                w.align()
                shifted(0)
                shifted(1)
                conv_inputs()
                key_norm()
                conv_gate(0)
                shifted(2)
                bias_of(0)
                for j in range(4):
                    decay(j)
                with w.loop("mix", KT - 1, uses("mix", l, "act")) as i:
                    chunks(i, True)
                chunks(KT - 1, False)

            def attend(l, lo):
                with w.loop("attend", KV, uses("attend", l, "act")) as i:
                    for u in range(2):
                        act.wait_ge(*A.full())
                        o = A_bank()
                        act.activation(qs[:, u, lo:T], o[:, lo:T], ACT.Copy, scale=ATT_SCALE).then_inc(A.free, 1)
                    for u in range(2):
                        for hh in range(2):
                            r = slice(64 * hh, 64 * hh + 64)
                            for seg in range(lo // SEG, 2):
                                nk = SEG if seg == 0 else T
                                for j in range(2):
                                    act.wait_ge(*E["max_ready"].next())
                                    act.activation(pr[:, j, 0:nk], sc[:, j, 0:nk], ACT.Exp,
                                                   bias=st[:, 8 * j + 1:8 * j + 2], accum_out=st[:, 8 * j + 2:8 * j + 3])
                                    act.activation(st[:, 8 * j + 3:8 * j + 4], sinkc[:, 2 * u + hh:2 * u + hh + 1],
                                                   ACT.Exp, bias=st[:, 8 * j + 1:8 * j + 2])\
                                       .then_inc(ev["exp_ready"], 1)
                                for j in range(2):
                                    act.wait_ge(*A.full())
                                    o = A_bank()
                                    act.copy(pT[:, 0:nk // P, j * P:(j + 1) * P],
                                             o[:, 0:nk].rearrange("p (k t) -> p k t", t=P)).then_inc(A.free, 1)
                                act.wait_ge(*A.full())
                                o = A_bank()
                                act.copy(yC[r, bass.ds(i * 2 + u, 1), seg * SEG:(seg + 1) * SEG],
                                         o[r, 0:SEG].unsqueeze(1)).then_inc(A.free, 1)

            for l in range(DEPTH):
                lo = 0 if l < DEPTH - 1 else SEG
                phase()
                if l == 0:
                    act.wait_ge(*E["silu_in"].next())
                    act.activation(crow[:, 0:2 * KT], ct[:, :], ACT.Tanh, scale=0.5).then_inc(ev["tanh_ready"], 1)
                phase()
                phase()
                norm(0)
                phase()
                act.wait_ge(*A.full())
                o = A_bank()
                act.activation(low[:, 0, :], o, ACT.Tanh).then_inc(A.free, 1)
                act.wait_ge(*A.full())
                o = A_bank()
                act.copy(low[:, 1, :], o).then_inc(A.free, 1)
                act.wait_ge(*A.full())
                o = A_bank()
                act.activation(low[:, 2, :], o, ACT.Tanh, scale=0.5).then_inc(A.free, 1)
                act.wait_ge(*A.freed())
                act.activation(low[:, 2, :], low[:, 2, :], ACT.Copy, bias=0.5, scale=0.5).then_inc(s_act, 1)
                act.wait_ge(*order.next())
                phase()
                mix(l, lo)
                phase()
                for q in range(2):
                    act.wait_ge(*A.full())
                    o = A_bank()
                    act.copy(K1[:, q, :], o).then_inc(A.free, 1)
                for q in range(2):
                    act.wait_ge(*A.full())
                    o = A_bank()
                    act.copy(VT[:, :, q * P:(q + 1) * P], o.rearrange("p (j t) -> p j t", j=4)).then_inc(A.free, 1)
                phase()
                phase()
                attend(l, lo)
                phase()
                with w.loop("merge", KT, uses("merge", l, "act")) as i:
                    for y in range(3):
                        act.wait_ge(*A.full())
                        o = A_bank()
                        act.activation(sg[:, y, lo:T], o[:, lo:T], ACT.Tanh, scale=0.5).then_inc(A.free, 1)
                    act.wait_ge(*E["merged"].next())
                phase()
                phase()
                norm(lo)
                phase()
                with w.loop("up", FT // 2, uses("up", l, "act")) as i:
                    for j in range(2):
                        for q in range(2):
                            act.wait_ge(*uf.free())
                            b = uf.last[0]
                            act.wait_ge(*A.full())
                            o = A_bank()
                            act.copy(upp[:, b, lo // SEG:, 1:SEG + 1],
                                     o[:, lo:T].rearrange("p (s t) -> p s t", t=SEG)).then_inc(A.free, 1)
                        act.wait_ge(*E["silu_in"].next())
                        act.activation(upt[:, 0, lo:T], upc[:, 0, lo:T], ACT.Tanh, scale=0.5)\
                           .then_inc(ev["tanh_ready"], 1)
                phase()
                phase()
            norm(SEG)
            phase()

        @block.vector
        def _(dve):
            w = Worker(dve)
            V = Empty(w, forD)
            WA, WG = Watch(w, forA), Watch(w, forG)
            ur = Release(w, up_buf)
            E = {n: Event(w, ev[n], n) for n in (
                "kk_sq_ready", "rinv_ready", "cum_ready", "powers_ready", "hats_ready", "v_ready", "bonus_ready",
                "inverse_ready", "y_ready", "devsq_ready", "state_ready", "rs_ready", "head_ready", "max_ready",
                "exp_ready", "prob_ready", "silu_in", "tanh_ready", "merged")}
            order = Event(w, s_vec, "vec_order")
            phase = Phases(dve)
            tt, ts, stt = dve.tensor_tensor, dve.tensor_scalar, dve.scalar_tensor_tensor
            MUL, ADD = ALU.mult, ALU.add
            dve.wait_ge(s_tab, 16)

            def V_bank():
                return PS[:, BANK_D[V.last[0]], :]

            def seg2(v):
                return v.rearrange("p (s t) -> p s t", t=SEG)

            def over(mask, n):
                return mask.unsqueeze(1).broadcast_to([P, n, mask.shape[1]])

            def norm(lo, g, shift, last=False):
                for k in range(KT):
                    tt(sq[:, k, lo:T], xT[:, k, lo:T], xT[:, k, lo:T], MUL).then_inc(ev["sq_ready"], 1)
                if not last:
                    for j in range(2):
                        stt(gs[:, :, j], mod[:, shift + KT:shift + 2 * KT, j], 1.0, g, ADD, MUL).then_inc(s_vec, 1)
                        dve.wait_ge(*order.next())
                dve.wait_ge(*E["rs_ready"].next())
                for k in range(KT):
                    ins = tt(hT[:, k, lo:T], xT[:, k, lo:T], rs[:, lo:T], MUL)
                ins.then_inc(s_vec, 1)
                dve.wait_ge(*order.next())
                for k in range(KT):
                    for s in range(lo // SEG, 2):
                        v, j = hT[:, k, s * SEG:(s + 1) * SEG], 1 - s
                        if last:
                            ins = ts(v, v, g[:, k:k + 1], None, MUL)
                        else:
                            ins = ts(v, v, gs[:, k, j:j + 1], mod[:, shift + k, j:j + 1], MUL, ADD)
                ins.then_inc(s_vec, 1)
                dve.wait_ge(*order.next())

            def setup(l):
                dve.wait_ge(*V.full())
                dve.tensor_copy(pp[:, 0:16, :].rearrange("p g c -> p (g c)"), V_bank()[:, 0:P]).then_inc(V.free, 1)
                dve.wait_ge(*V.freed())
                dve.wait_ge(*V.full())
                dve.tensor_copy(pb[:, :], V_bank()[:, 0:88]).then_inc(V.free, 1)
                dve.wait_ge(*V.full())
                dve.tensor_copy(pf[:, 0:P], V_bank()[:, 0:P]).then_inc(V.free, 1)
                dve.wait_ge(*V.full())
                dve.tensor_copy(pf[:, P:P + 4], V_bank()[:, 0:4]).then_inc(V.free, 1)
                tt(pp[:, 16:19, :], pp[:, 0:3, :], pp[:, 3:6, :], ADD).then_inc(s_vec, 1)
                dve.wait_ge(*order.next())
                ts(pp[:, 16:19, :], pp[:, 16:19, :], -1.0, 1.0, MUL, ADD).then_inc(s_vec, 1)
                dve.wait_ge(*order.next())
                ts(pp[:, 19:21, :], pp[:, 6:8, :], 0.5, None, MUL).then_inc(s_vec, 1)
                dve.wait_ge(*order.next())
                ts(pp[:, 21:23, :], pp[:, 8:10, :], 0.5, None, MUL).then_inc(s_vec, 1)
                dve.wait_ge(*order.next())
                ts(pp[:, 23, :], pp[:, 11, :], -1.0, 1.0, MUL, ADD).then_inc(s_vec, 1)
                dve.wait_ge(*order.next())
                if l == 0:
                    dve.wait_ge(*V.full())
                    dve.tensor_copy(ct[:, :], V_bank()[:, 0:2 * KT]).then_inc(V.free, 1)
                    dve.wait_ge(*V.freed())
                    dve.tensor_copy(ct[:, :], ct[:, :]).then_inc(ev["silu_in"], 1)
                    dve.wait_ge(*E["silu_in"].next())
                    dve.wait_ge(*E["tanh_ready"].next())
                    stt(ct[:, :], crow[:, 0:2 * KT], 1.0, ct[:, :], ADD, MUL).then_inc(s_vec, 1)
                    dve.wait_ge(*order.next())
                    ts(cT[:, :, :], ct.rearrange("p (j k) -> p k j", j=2), 0.5, None, MUL).then_inc(s_vec, 1)
                    dve.wait_ge(*order.next())
                    for k in range(KT):
                        dve.wait_ge(*V.full())
                        dve.tensor_copy(xT[:, k, :], V_bank()).then_inc(V.free, 1)

            def conv(dst, src, g0, g1, g2, release=None, last=None):
                n = SEG
                ts(dst, src[:, :, 1:n + 1], g1, None, MUL).then_inc(s_vec, 1)
                dve.wait_ge(*order.next())
                stt(dst, src[:, :, 0:n], g0, dst, MUL, ADD).then_inc(s_vec, 1)
                dve.wait_ge(*order.next())
                ins = stt(dst, src[:, :, 2:n + 2], g2, dst, MUL, ADD)
                if release is not None:
                    ins.then_inc(release.free(), 1)
                    dve.wait_ge(*release.freed())
                elif last is not None:
                    ins.then_inc(last.sem, 1)
                    dve.wait_ge(*last.next())
                else:
                    ins.then_inc(s_vec, 1)
                    dve.wait_ge(*order.next())

            def mix(l, lo):
                s0, c0 = lo // SEG, lo // P
                for v in (rkvp[:, 0], rkvp[:, 1], rkvp[:, 2], axp):
                    dve.memset(v[:, :, 0:1], 0.0).then_inc(s_vec, 1)
                    dve.wait_ge(*order.next())
                    dve.memset(v[:, :, SEG + 1:SEG + 2], 0.0).then_inc(s_vec, 1)
                    dve.wait_ge(*order.next())
                def g(n):
                    return pc[:, n:n + 1]

                r, k, v = rkv[:, 0, :], rkv[:, 1, :], rkv[:, 2, :]

                def shift_r_and_k(i):
                    dve.tensor_copy(pc[:, 0:24].unsqueeze(2), pp[:, :, bass.ds(i, 1)]).then_inc(s_vec, 1)
                    dve.wait_ge(*order.next())
                    dve.tensor_copy(pc[:, 24:27].unsqueeze(2),
                                    pb[:, 0:24].rearrange("p (w k) -> p w k", w=3)[:, :, bass.ds(i, 1)]).then_inc(s_vec, 1)
                    dve.wait_ge(*order.next())
                    for q in range(2):
                        dve.wait_ge(*WG.next())
                        conv(seg2(rkv[:, q, :]), rkvp[:, q], g(q), g(16 + q), g(3 + q))

                def shift_v():
                    dve.wait_ge(*WG.next())
                    conv(seg2(v), rkvp[:, 2], g(2), g(18), g(5), last=E["v_ready"])

                def key_squares():
                    ts(kk, k, g(10), None, MUL).then_inc(s_vec, 1)
                    dve.wait_ge(*order.next())
                    tt(t1, kk, kk, MUL).then_inc(ev["kk_sq_ready"], 1)
                    dve.wait_ge(*E["kk_sq_ready"].next())

                def decays():
                    for _ in range(4):
                        dve.wait_ge(*WA.next())
                    ts(th[:, 0:2, :], th[:, 0:2, :], -0.5 * DECAY, -0.5 * DECAY, MUL, ADD).then_inc(s_vec, 1)
                    dve.wait_ge(*order.next())
                    ts(th[:, 2:4, :], th[:, 2:4, :], 0.5, 0.5, MUL, ADD).then_inc(s_vec, 1)
                    dve.wait_ge(*order.next())

                def short_conv():
                    dve.wait_ge(*WG.next())
                    dve.wait_ge(*WG.next())
                    x = axp[:, s0:, 1:SEG + 1]
                    tt(x, x, seg2(acb[:, lo:T]), MUL).then_inc(s_vec, 1)
                    dve.wait_ge(*order.next())
                    conv(seg2(ysum[:, lo:T]), axp[:, s0:], g(24), g(25), g(26))

                def conv_out(i):
                    dve.wait_ge(*WG.next())
                    y = yA[:, bass.ds(i, 1), lo:T]
                    tt(y, ysum[:, lo:T].unsqueeze(1), y, MUL).then_inc(s_vec, 1)
                    dve.wait_ge(*order.next())

                def normed_key():
                    WG.skip()
                    dve.wait_ge(*E["rinv_ready"].next())
                    tt(kk, kk, rinv, MUL).then_inc(s_vec, 1)
                    dve.wait_ge(*order.next())

                def chunks(i, ahead):
                    for d in range(2):
                        ld, av = th[:, d, :], th[:, 2 + d, :]
                        back = slice(None, None, -1) if d else slice(None)
                        dve.tensor_tensor_scan(cum[:, back], tab["restart"], ld[:, back], 0.0, MUL, ADD).then_inc(s_vec, 1)
                        dve.wait_ge(*order.next())
                        tt(t1, cum, ld, ALU.subtract).then_inc(ev["cum_ready"], 1)
                        dve.wait_ge(*E["cum_ready"].next())
                        ts(t2, av, g(11), g(23), MUL, ADD).then_inc(s_vec, 1)
                        dve.wait_ge(*order.next())
                        tt(kd[:, d, :], t2, k, MUL).then_inc(s_vec, 1)
                        dve.wait_ge(*order.next())
                        tt(t2, kk, av, MUL).then_inc(s_vec, 1)
                        dve.wait_ge(*order.next())
                        dve.wait_ge(*E["powers_ready"].next())

                        stt(AR[d][:, 0, :], kk, -1.0, Pe, MUL, MUL)
                        tt(AR[d][:, 1, :], r, Pi, MUL)
                        dve.tensor_copy(AR[d][:, 2, :].rearrange("p (c t) -> p c t", t=CH), over(tab["eye64"], NCH))
                        tt(BT[d], t2, Pn, MUL)
                        tt(KTr[d], kd[:, d, :], Pn, MUL).then_inc(ev["hats_ready"], 1)
                        dve.wait_ge(*E["hats_ready"].next())
                    tt(t1, kd[:, 0, :], kd[:, 1, :], ADD).then_inc(s_vec, 1)
                    dve.wait_ge(*order.next())
                    stt(t2, t1, g(12), r, MUL, MUL).then_inc(ev["bonus_ready"], 1)
                    dve.wait_ge(*E["bonus_ready"].next())
                    for d in range(2):
                        both = C[:, at[f"strict{d}"][0]:at[f"strict{d}"][0] + 2 * CH]
                        for dst in (LB, MK):
                            for h in range(2):
                                dve.wait_ge(*V.full())
                                o = V_bank()
                                tt(dst[d][:, 4 * h:4 * h + 4, 0:2, :].rearrange("p q j t -> p q (j t)"),
                                   o.rearrange("p (q j) -> p q j", q=4), over(both, 4), MUL).then_inc(V.free, 1)
                                dve.wait_ge(*V.freed())
                        for h in range(2):
                            dve.wait_ge(*V.full())
                            o = V_bank()
                            tt(TT[d][:, 4 * h:4 * h + 4, :],
                               o[:, 0:4 * CH].rearrange("p (q j) -> p q j", q=4),
                               over(tab[f"level{d}0"], 4), MUL).then_inc(V.free, 1)
                            dve.wait_ge(*V.freed())
                        tt(TT[d], TT[d], over(tab["eye64"], NCH), ADD).then_inc(s_vec, 1)
                        dve.wait_ge(*order.next())
                        tt(ZZ[d], LB[d][:, :, 0, :], over(tab[f"level{1 - d}0"], NCH), MUL).then_inc(s_vec, 1)
                        dve.wait_ge(*order.next())
                        tt(ZZ[d], ZZ[d], over(tab["eye64"], NCH), ADD).then_inc(ev["inverse_ready"], 1)
                        dve.wait_ge(*E["inverse_ready"].next())
                    dve.wait_ge(*V.full())
                    o = V_bank()
                    tt(bon[:, lo:T], o[:, lo:T], v[:, lo:T], MUL).then_inc(V.free, 1)

                    def eight(x):
                        return x.rearrange("p (q t) -> p q t", q=NCH)

                    dve.tensor_copy(pg[:, :], pc[:, 13:15]).then_inc(s_vec, 1)
                    dve.wait_ge(*order.next())
                    for j in range(1, LEVELS + 1):
                        for d in range(2):
                            dve.wait_ge(*V.full())
                            o = V_bank()
                            tt(XX[d], eight(o), over(tab[f"level{d}{j}"], NCH), MUL).then_inc(V.free, 1)
                        for d in range(2):
                            if j < LEVELS:
                                dve.wait_ge(*V.full())
                                o = V_bank()
                                tt(TT[d], eight(o), TT[d], ADD).then_inc(V.free, 1)
                            dve.wait_ge(*V.full())
                            o = V_bank()
                            tt(ZZ[d], eight(o), ZZ[d], ADD).then_inc(V.free, 1)
                            if j == LEVELS:
                                dve.wait_ge(*V.freed())
                        if j == 1:
                            WA.skip(8)
                        if ahead and j == 1:
                            shift_r_and_k(i + 1)
                            key_squares()
                        if j == 2:
                            if ahead:
                                WA.skip(2)
                                decays()
                            else:
                                WA.skip(2)
                        if ahead and j == 3:
                            short_conv()
                        if ahead and j == LEVELS:
                            normed_key()
                            conv_out(i + 1)
                    for d in range(2):
                        for p in range(2):
                            dve.wait_ge(*V.full())
                            o = V_bank()
                            mine = AR[d][:, 1:3, :].rearrange("p j (c q t) -> p c q j t", q=2, t=CH)[:, :, p]
                            tt(mine, o.rearrange("p (c j t) -> p c j t", c=4, j=2), mine, ADD).then_inc(V.free, 1)
                        for p in range(2):
                            dve.wait_ge(*V.full())
                            o = V_bank()
                            tt(CC[d].rearrange("p (c q) t -> p c q t", q=2)[:, :, p, :],
                               o[:, 0:4 * CH].rearrange("p (c t) -> p c t", c=4),
                               PC[:, d, p:NCH:2].unsqueeze(2).broadcast_to([P, 4, CH]), MUL).then_inc(V.free, 1)
                            dve.wait_ge(*V.freed())
                    dve.memset(GG[0][:, ORDER[0][0], :], 0.0).then_inc(s_vec, 1)
                    dve.wait_ge(*order.next())
                    dve.memset(GG[1][:, ORDER[1][0], :], 0.0).then_inc(ev["state_ready"], 1)
                    dve.wait_ge(*E["state_ready"].next())
                    for s in range(NCH - 1):
                        for d in range(2):
                            c, n = ORDER[d][s], ORDER[d][s + 1]
                            dve.wait_ge(*V.full())
                            o = V_bank()
                            stt(GG[d][:, n, :], o[:, 0:CH], PC[:, d, c:c + 1], CC[d][:, c, :], MUL, ADD).then_inc(V.free, 1)
                    WA.skip(4)
                    dve.wait_ge(*WA.next())
                    dve.wait_ge(*WA.next())
                    dve.wait_ge(*V.full())
                    o = V_bank()
                    tt(ysum[:, lo:T], ysum[:, lo:T], o[:, lo:T], ADD).then_inc(V.free, 1)
                    dve.wait_ge(*V.freed())
                    dve.tensor_copy(pc[:, 0:1], pc[:, 0:1]).then_inc(ev["y_ready"], 1)
                    dve.wait_ge(*E["y_ready"].next())
                    if ahead:
                        shift_v()
                    WA.skip()
                    dve.wait_ge(*V.full())
                    o = V_bank()
                    stt(t2[:, lo:T], o[:, lo:T], -1.0 / HD, ysum[:, lo:T], MUL, ADD).then_inc(V.free, 1)
                    dve.wait_ge(*V.freed())
                    tt(t1[:, lo:T], t2[:, lo:T], t2[:, lo:T], MUL).then_inc(ev["devsq_ready"], 1)
                    dve.wait_ge(*E["devsq_ready"].next())
                    dve.wait_ge(*E["rinv_ready"].next())
                    tt(t2[:, lo:T], t2[:, lo:T], rinv[:, lo:T], MUL).then_inc(s_vec, 1)
                    dve.wait_ge(*order.next())
                    ts(t2[:, lo:T], t2[:, lo:T], pg[:, 0:1], pg[:, 1:2], MUL, ADD).then_inc(s_vec, 1)
                    dve.wait_ge(*order.next())
                    tt(t2[:, lo:T], t2[:, lo:T], bon[:, lo:T], ADD).then_inc(s_vec, 1)
                    dve.wait_ge(*order.next())
                    tt(yB[:, bass.ds(i, 1), lo:T], t2[:, lo:T].unsqueeze(1), gb[:, lo:T].unsqueeze(1), MUL)\
                        .then_inc(s_vec, 1)
                    dve.wait_ge(*order.next())

                w.align()
                shift_r_and_k(0)
                key_squares()
                short_conv()
                normed_key()
                conv_out(0)
                shift_v()
                decays()
                with w.loop("mix", KT - 1, uses("mix", l, "dve")) as i:
                    chunks(i, True)
                chunks(KT - 1, False)

            def rope(v, o):
                tt(rot_t, o[:, 0:SEG], tab["sin"], MUL).then_inc(V.free, 1)
                dve.wait_ge(*V.freed())
                tt(cos_t, v, tab["cos"], MUL).then_inc(s_vec, 1)
                dve.wait_ge(*order.next())
                tt(v, cos_t, rot_t, ADD).then_inc(s_vec, 1)
                dve.wait_ge(*order.next())

            def attend(l, lo):
                with w.loop("attend", KV, uses("attend", l, "dve")) as i:
                    WA.skip(2 + 12 * (2 - lo // SEG))
                    for u in range(2):
                        dve.wait_ge(*V.full())
                        rope(qs[:, u, SEG:T], V_bank())
                    dve.tensor_copy(kcur.unsqueeze(1), K2[:, bass.ds(i, 1), :]).then_inc(s_vec, 1)
                    dve.wait_ge(*order.next())
                    dve.tensor_copy(vcur, VT[:, :, bass.ds(i * HD, HD)]).then_inc(s_vec, 1)
                    dve.wait_ge(*order.next())
                    dve.tensor_copy(sinkc, sink[:, l, bass.ds(i * 4, 4)]).then_inc(ev["head_ready"], 1)
                    dve.wait_ge(*E["head_ready"].next())
                    for u in range(2):
                        for hh in range(2):
                            for seg in range(lo // SEG, 2):
                                nk = SEG if seg == 0 else T
                                for j in range(2):
                                    dve.wait_ge(*V.full())
                                    o = V_bank()
                                    if seg:
                                        tt(sc[:, j, :], o, win[:, j, :], ADD).then_inc(V.free, 1)
                                        dve.wait_ge(*V.freed())
                                    else:
                                        dve.tensor_copy(sc[:, j, 0:nk], o[:, 0:nk]).then_inc(V.free, 1)
                                        dve.wait_ge(*V.freed())
                                    s = 8 * j
                                    dve.tensor_reduce(st[:, s:s + 1], sc[:, j, 0:nk], AX_X, ALU.max).then_inc(s_vec, 1)
                                    dve.wait_ge(*order.next())
                                    ts(st[:, s + 1:s + 2], st[:, s:s + 1],
                                       sinkc[:, 2 * u + hh:2 * u + hh + 1], -1.0, ALU.max, MUL).then_inc(ev["max_ready"], 1)
                                    dve.wait_ge(*E["max_ready"].next())
                                for j in range(2):
                                    s = 8 * j
                                    dve.wait_ge(*E["exp_ready"].next())
                                    tt(st[:, s + 4:s + 5], st[:, s + 2:s + 3], st[:, s + 3:s + 4], ADD).then_inc(s_vec, 1)
                                    dve.wait_ge(*order.next())
                                    dve.reciprocal(st[:, s + 5:s + 6], st[:, s + 4:s + 5]).then_inc(s_vec, 1)
                                    dve.wait_ge(*order.next())
                                    ts(pr[:, j, 0:nk], pr[:, j, 0:nk], st[:, s + 5:s + 6],
                                       None, MUL).then_inc(ev["prob_ready"], 1)
                                    dve.wait_ge(*E["prob_ready"].next())

            def residual(o, k, lo, gate):
                for s in range(lo // SEG, 2):
                    v = xT[:, bass.ds(k, 1), s * SEG:(s + 1) * SEG]
                    ins = stt(v, o[:, s * SEG:(s + 1) * SEG].unsqueeze(1), gate(k, 1 - s), v, MUL, ADD)
                    if s == 1:
                        ins.then_inc(V.free, 1)
                        dve.wait_ge(*V.freed())

            for l in range(DEPTH):
                lo = 0 if l < DEPTH - 1 else SEG
                s0 = lo // SEG
                phase()
                setup(l)
                phase()
                with w.loop("ada", 6, {"psum_vec": 2}) as i:
                    for j in range(2):
                        dve.wait_ge(*V.full())
                        o = V_bank()
                        m = bass.ds(i * 8 + 4 * j, 4)
                        tt(mod[:, m, :], o[:, 0:8].rearrange("p (m j) -> p m j", j=2),
                           pb[:, 32:80][:, m].unsqueeze(2).broadcast_to([P, 4, 2]), ADD).then_inc(V.free, 1)
                phase()
                ts(gh[:, :, :], mod[:, 2 * KT:3 * KT, :], 0.5, None, MUL).then_inc(s_vec, 1)
                dve.wait_ge(*order.next())
                norm(0, pp[:, 15, :], 0)
                WA.skip()
                phase()
                WA.skip(3)
                phase()
                mix(l, lo)
                phase()
                WA.skip(4)
                for q in range(2):
                    dve.wait_ge(*V.full())
                    rope(K1[:, q, SEG:T], V_bank())
                phase()
                phase()
                attend(l, lo)
                phase()
                with w.loop("merge", KT, uses("merge", l, "dve")) as i:
                    for y in range(3):
                        dve.wait_ge(*WA.next())
                        dve.wait_ge(*V.full())
                        o = V_bank()
                        stt(mt[:, min(y, 1), lo:T], sg[:, y, lo:T], 1.0, o[:, lo:T], ADD, MUL).then_inc(V.free, 1)
                        dve.wait_ge(*V.freed())
                        if y == 1:
                            tt(mt[:, 0, lo:T], mt[:, 0, lo:T], mt[:, 1, lo:T], ADD).then_inc(s_vec, 1)
                            dve.wait_ge(*order.next())
                    tt(mT[:, bass.ds(i, 1), lo:T], mt[:, 0, lo:T].unsqueeze(1),
                       mt[:, 1, lo:T].unsqueeze(1), ADD).then_inc(ev["merged"], 1)
                    dve.wait_ge(*E["merged"].next())
                phase()
                with w.loop("w_o", KT // 4, {"psum_vec": 4}) as i:
                    for j in range(4):
                        dve.wait_ge(*V.full())
                        residual(V_bank(), i * 4 + j, lo, lambda k, s: gh[:, bass.ds(k, 1), s])
                phase()
                norm(lo, pb[:, 24:32], 3 * KT)
                WA.skip()
                phase()
                for b in range(4):
                    dve.memset(upp[:, b, :, 0:1], 0.0).then_inc(s_vec, 1)
                    dve.wait_ge(*order.next())
                    dve.memset(upp[:, b, :, SEG + 1:SEG + 2], 0.0).then_inc(s_vec, 1)
                    dve.wait_ge(*order.next())
                with w.loop("up", FT // 2, uses("up", l, "dve")) as i:
                    for j in range(2):
                        f = pfc[:, j, :]
                        dve.tensor_copy(f.rearrange("p (a b) -> p a b", a=3).unsqueeze(3),
                                        pf[:, :].rearrange("p (w g k) -> p w g k", w=3, g=2)[:, :, :, bass.ds(i * 2 + j, 1)]).then_inc(s_vec, 1)
                        dve.wait_ge(*order.next())
                        for q in range(2):
                            dve.wait_ge(*WA.next())
                            conv(seg2(upc[:, q, lo:T]), upp[:, 2 * j + q, s0:], f[:, q:q + 1], f[:, 2 + q:3 + q],
                                 f[:, 4 + q:5 + q], release=ur)
                            if q == 0:
                                dve.tensor_copy(f[:, 0:1], f[:, 0:1]).then_inc(ev["silu_in"], 1)
                                dve.wait_ge(*E["silu_in"].next())
                        dve.wait_ge(*E["tanh_ready"].next())
                        stt(upt[:, 1, lo:T], upt[:, 0, lo:T], 1.0, upc[:, 0, lo:T], ADD, MUL).then_inc(s_vec, 1)
                        dve.wait_ge(*order.next())
                        stt(hid[:, bass.ds(i * 2 + j, 1), lo:T], upt[:, 1, lo:T].unsqueeze(1), 0.5,
                            upc[:, 1, lo:T].unsqueeze(1), MUL, MUL).then_inc(s_vec, 1)
                        dve.wait_ge(*order.next())
                phase()
                with w.loop("down", KT, {"psum_vec": 1}) as i:
                    dve.wait_ge(*V.full())
                    residual(V_bank(), i, lo, lambda k, s: mod[:, 5 * KT:6 * KT, s][:, bass.ds(k, 1)])
                phase()
            norm(SEG, pb[:, 80:88], 0, True)
            WA.skip()
            dve.tensor_copy(pc[:, 0:1], pc[:, 0:1]).then_inc(ev["y_ready"], 1)
            dve.wait_ge(*E["y_ready"].next())
            for j in range(2):
                for half in range(2):
                    dve.wait_ge(*V.full())
                    dve.tensor_copy(yout[:, j, half * 512:(half + 1) * 512], V_bank()).then_inc(V.free, 1)
            phase()


_INS = ['x', 'c', 'ctx', 'c_ctx', 'ada_w', 'ada_b', 'norm1_g', 'w_in', 'conv_a_w', 'a_out_w', 'rwkv_mu', 'rwkv_w0',
        'rwkv_w2', 'rwkv_a0', 'rwkv_a2', 'rwkv_g2', 'rwkv_k_k', 'rwkv_k_a', 'rwkv_r_k', 'rwkv_ln_g', 'rwkv_ln_b',
        'rwkv_out_w', 'attn_sink', 'attn_out_w', 'w_o', 'norm2_g', 'ffn_up', 'ffn_conv', 'ffn_down', 'final_norm_g']


def program(nc, shapes):
    args = {n: nc.dram_tensor(f"in_{n}_dram", s, F32, kind="ExternalInput").ap() for n, s in shapes.items()}
    table, at = constants()
    consts = nc.dram_tensor("tables_dram", table.shape, F32, kind="ExternalInput").ap()
    window = nc.dram_tensor("window_dram", (P, 2 * T), F32, kind="ExternalInput").ap()
    x_scratch = nc.dram_tensor("x_scratch", (P, KT * T), F32, kind="Internal").ap()
    out = nc.dram_tensor("out_0_dram", (1, SEG, D), F32, kind="ExternalOutput").ap()
    trunk(nc, args, consts, window, x_scratch, out, at)
    return {"tables_dram": table, "window_dram": window_table().reshape(P, 2 * T)}


def kernel(**inputs):
    import concourse.bacc as bacc
    from concourse.bass_utils import run_bass_kernel_spmd

    nc = bacc.Bacc("TRN2", target_bir_lowering=False, num_devices=1)
    arrays = {n: np.ascontiguousarray(inputs[n]) for n in _INS}
    tables = program(nc, {n: v.shape for n, v in arrays.items()})
    ins = {f"in_{n}_dram": v for n, v in arrays.items()} | tables
    r = run_bass_kernel_spmd(nc, [ins], core_ids=[0])
    return r.results[0]["out_0_dram"]
```
